# Optimizing a Trainium2 kernel written in Bass

```python
import math
import jax, jax.numpy as jnp
from jax import lax
import numpy as np

D_MODEL = 2048
BATCH = 1
SEQ = 256
DEPTH = 2

CHUNK = 64
N_A_LAYERS = DEPTH // 2
N_B_LAYERS = DEPTH - N_A_LAYERS
POOL_WINDOWS = (2, 4, 8, 16)
N_POOL_GROUPS = len(POOL_WINDOWS)
POOL_GROUP = D_MODEL // N_POOL_GROUPS
N_HEADS = 8
HEAD_DIM = D_MODEL // (2 * N_HEADS)
V_HEAD_DIM = 2 * HEAD_DIM
ROT_DIM = HEAD_DIM // 4
ROPE_THETA = 500000.0
D_FF = 4 * D_MODEL
Q_BLOCK = 128
EPS = 1e-6

kernel_name = "yoco_pool_diffattn_encoder"

def rms_norm(x, g):
    xf = x.astype(jnp.float32)
    y = xf * lax.rsqrt(jnp.mean(xf * xf, axis=-1, keepdims=True) + EPS)
    return (y * g.astype(jnp.float32)).astype(x.dtype)

def rope_tables(seq):
    pos = jnp.arange(seq, dtype=jnp.float32)
    inv_freq = ROPE_THETA ** (-jnp.arange(0, ROT_DIM, 2, dtype=jnp.float32) / ROT_DIM)
    ang = pos[:, None] * inv_freq[None, :]
    return jnp.cos(ang), jnp.sin(ang)

def apply_partial_rope(t, cos, sin):
    half = ROT_DIM // 2
    r1 = t[..., :half]
    r2 = t[..., half:ROT_DIM]
    keep = t[..., ROT_DIM:]
    c = cos[None, :, None, None, :].astype(t.dtype)
    s = sin[None, :, None, None, :].astype(t.dtype)
    return jnp.concatenate([r1 * c - r2 * s, r2 * c + r1 * s, keep], axis=-1)

def multiscale_pool_mixer(h, w_pool, scale):
    b, s, d = h.shape
    hf = h.astype(jnp.float32)
    t = jnp.arange(1, s + 1, dtype=jnp.float32)
    groups = []
    for g, w in enumerate(POOL_WINDOWS):
        hg = hf[..., g * POOL_GROUP:(g + 1) * POOL_GROUP]
        cs = jnp.cumsum(hg, axis=1)
        lagged = jnp.pad(cs, ((0, 0), (w, 0), (0, 0)))[:, :s]
        cnt = jnp.minimum(t, float(w))[None, :, None]
        groups.append((cs - lagged) / cnt - hg)
    pooled = jnp.stack(groups, axis=2).astype(h.dtype)
    y = jnp.einsum('bsgc,gce->bsge', pooled, w_pool).reshape(b, s, d)
    return y * scale

def shared_kv(x, g, w_kv, cos, sin):
    b, s, _ = x.shape
    h = rms_norm(x, g)
    kv = h @ w_kv
    k = kv[..., :D_MODEL].reshape(b, s, N_HEADS, 2, HEAD_DIM)
    v = kv[..., D_MODEL:].reshape(b, s, N_HEADS, V_HEAD_DIM)
    return apply_partial_rope(k, cos, sin), v

def diff_attention(h, k, v, w_q, lam, subln_g, w_o, cos, sin, layer_idx):
    b, s, _ = h.shape
    q = (h @ w_q).reshape(b, s, N_HEADS, 2, HEAD_DIM)
    q = apply_partial_rope(q, cos, sin)
    lam_init = 0.8 - 0.6 * math.exp(-0.3 * layer_idx)
    lamf = lam.astype(jnp.float32)
    lam_full = (jnp.exp(jnp.sum(lamf[0] * lamf[1]))
                - jnp.exp(jnp.sum(lamf[2] * lamf[3])) + lam_init)
    sm_scale = HEAD_DIM ** -0.5
    chunk_k = jnp.arange(s) // CHUNK
    vf = v.astype(jnp.float32)
    neg = jnp.finfo(jnp.float32).min

    def block(i):
        q0 = i * Q_BLOCK
        qb = lax.dynamic_slice_in_dim(q, q0, Q_BLOCK, axis=1)
        sc = jnp.einsum('bqhcd,bkhcd->bhcqk', qb, k,
                        preferred_element_type=jnp.float32) * sm_scale
        chunk_q = (q0 + jnp.arange(Q_BLOCK)) // CHUNK
        visible = chunk_k[None, :] <= chunk_q[:, None]
        sc = jnp.where(visible, sc, neg)
        p = jax.nn.softmax(sc, axis=-1)
        a = p[:, :, 0] - lam_full * p[:, :, 1]
        return jnp.einsum('bhqk,bkhe->bqhe', a, vf)

    o = lax.map(block, jnp.arange(s // Q_BLOCK))
    o = jnp.moveaxis(o, 0, 1).reshape(b, s, N_HEADS, V_HEAD_DIM)
    o = rms_norm(o, subln_g) * (1.0 - lam_init)
    return o.reshape(b, s, D_MODEL).astype(h.dtype) @ w_o

def sqrelu_mlp(h, w_in, w_out):
    u = jax.nn.relu(h @ w_in)
    return (u * u) @ w_out

def setup_inputs(seed: int = 0) -> dict:
    key = jax.random.key(seed)
    ks = jax.random.split(key, 16)
    f32 = jnp.float32
    nrm = lambda k, shape: jax.random.normal(k, shape, f32)
    x = nrm(ks[0], (BATCH, SEQ, D_MODEL))
    mix_norm = 1.0 + 0.02 * nrm(ks[1], (DEPTH, D_MODEL))
    mlp_norm = 1.0 + 0.02 * nrm(ks[2], (DEPTH, D_MODEL))
    pool_w = nrm(ks[3], (N_A_LAYERS, N_POOL_GROUPS, POOL_GROUP, POOL_GROUP)) * POOL_GROUP ** -0.5
    pool_scale = 1.0 + 0.02 * nrm(ks[4], (N_A_LAYERS, D_MODEL))
    kv_norm = 1.0 + 0.02 * nrm(ks[5], (D_MODEL,))
    w_kv = nrm(ks[6], (D_MODEL, 2 * D_MODEL)) * D_MODEL ** -0.5
    w_q = nrm(ks[7], (N_B_LAYERS, D_MODEL, D_MODEL)) * D_MODEL ** -0.5
    lam = 0.1 * nrm(ks[8], (N_B_LAYERS, 4, HEAD_DIM))
    subln = 1.0 + 0.02 * nrm(ks[9], (N_B_LAYERS, V_HEAD_DIM))
    w_o = nrm(ks[10], (N_B_LAYERS, D_MODEL, D_MODEL)) * D_MODEL ** -0.5
    w_mlp_in = nrm(ks[11], (DEPTH, D_MODEL, D_FF)) * D_MODEL ** -0.5
    w_mlp_out = nrm(ks[12], (DEPTH, D_FF, D_MODEL)) * D_FF ** -0.5
    final_norm = 1.0 + 0.02 * nrm(ks[13], (D_MODEL,))
    return {"x": x, "mix_norm": mix_norm, "mlp_norm": mlp_norm, "pool_w": pool_w,
            "pool_scale": pool_scale, "kv_norm": kv_norm, "w_kv": w_kv, "w_q": w_q,
            "lam": lam, "subln": subln, "w_o": w_o, "w_mlp_in": w_mlp_in,
            "w_mlp_out": w_mlp_out, "final_norm": final_norm}

def reference(x, mix_norm, mlp_norm, pool_w, pool_scale, kv_norm, w_kv, w_q, lam, subln,
              w_o, w_mlp_in, w_mlp_out, final_norm):
    s = x.shape[1]
    cos, sin = rope_tables(s)
    h = x
    k = None
    v = None
    for l in range(DEPTH):
        if l < N_A_LAYERS:
            h = h + multiscale_pool_mixer(rms_norm(h, mix_norm[l]), pool_w[l], pool_scale[l])
        else:
            j = l - N_A_LAYERS
            h = h + diff_attention(rms_norm(h, mix_norm[l]), k, v, w_q[j], lam[j], subln[j],
                                   w_o[j], cos, sin, l)
        h = h + sqrelu_mlp(rms_norm(h, mlp_norm[l]), w_mlp_in[l], w_mlp_out[l])
        if l == N_A_LAYERS - 1:
            k, v = shared_kv(h, kv_norm, w_kv, cos, sin)
    return rms_norm(h, final_norm)


_drawn_inputs = setup_inputs


def setup_inputs(seed=0):
    import zlib

    import numpy as np

    out = dict(_drawn_inputs(seed))
    spreads = {}
    factors = {'mix_norm': 3.575,
     'mlp_norm': 2.721,
     'pool_scale': 3.861,
     'kv_norm': 6.576,
     'subln': 7.792,
     'final_norm': 2.789}
    for name, (base, spread) in spreads.items():
        noise = np.random.default_rng([zlib.crc32(name.encode()), seed]).standard_normal(out[name].shape)
        drawn = base * np.exp(spread * noise) if base else spread * noise
        out[name] = __import__('jax').numpy.asarray(drawn.astype(out[name].dtype))
    for name, factor in factors.items():
        out[name] = (out[name] * factor).astype(out[name].dtype)
    return out
```

```python
import math
from contextlib import ExitStack

import numpy as np

import concourse.bass as bass
from concourse import mybir

F32 = mybir.dt.float32
F32R = mybir.dt.float32r
ACT = mybir.ActivationFunctionType
ALU = mybir.AluOpType
AX = mybir.AxisListType

P = 128
D = 2048
SEQ = 256
TB = SEQ // P
FF = 4 * D
SW = 512
NG = D // SW
HALVES = 2 * NG
RAW = 4
HEADS = 8
HD = 128
VD = 256
PAIRS = HEADS // 2
ROT = HD // 4
CHUNK = 64
WINDOWS = (2, 4, 8, 16)
REACH = P + max(WINDOWS)
EPS = 1e-6
SM_SCALE = HD ** -0.5
LAM_INIT = 0.8 - 0.6 * math.exp(-0.3 * 1)
MASKED = -3.0e38
NJ = FF // SW

S_POOL = 0
S_MLP = (1, 1 + 2 * NJ + 3 * PAIRS + PAIRS)
S_KV = 1 + 2 * NJ
S_Q = S_KV + 2 * PAIRS
S_O = S_Q + PAIRS
STRIPS = S_MLP[1] + 2 * NJ

H_POOL = 0
H_MLP = (NG, NG + NG * NJ + NG * PAIRS)
H_O = NG + NG * NJ

R_H = {0: 0, 1: NG + NJ}
R_U = {0: NG}
R_K = R_H[1] + NG
ATT = []
for _t in range(1, PAIRS + 3):
    if _t - 1 < PAIRS:
        ATT.append(("q", _t - 1))
    if _t - 3 >= 0:
        ATT.append(("o", _t - 3))
R_ATT = {what: R_K + PAIRS + n for n, what in enumerate(ATT)}
R_H[2] = R_K + PAIRS + len(ATT)
R_U[1] = R_H[2] + NG

X_H = {0: 0, 1: NG + NJ}
X_U = {0: NG}
X_O = X_H[1] + NG
X_H[2] = X_O + PAIRS
X_U[1] = X_H[2] + NG

C_IDENT, C_MASK, C_COS, C_SIN = 0, P, P + 384, P + 384 + TB * 4 * ROT
C_END = C_SIN + TB * 4 * ROT
C_BAND, C_COUNT = 0, 4 * 384
C_POOL_END = C_COUNT + 4 * SEQ

DVE_PIECES = [(0, slice(0, D // 2)), (0, slice(D // 2, D)), (1, slice(D // 2, D))]
ACT_PIECES = [(1, slice(0, D // 2))]

G_MIX, G_MLP, G_KV, G_SUB, G_ROWS = 0, 32, 64, 80, 82


def shape_constants():
    keep = np.zeros((P, C_END), np.float32)
    keep[:, C_IDENT:C_IDENT + P] = np.eye(P, dtype=np.float32)
    mask = np.zeros((P, 384), np.float32)
    mask[:CHUNK, CHUNK:P] = MASKED
    mask[:CHUNK, P + 192:P + 256] = MASKED
    keep[:, C_MASK:C_MASK + 384] = mask
    pos = np.arange(SEQ, dtype=np.float32)
    freq = np.float32(500000.0) ** (-np.arange(0, ROT, 2, dtype=np.float32) / np.float32(ROT))
    ang = (pos[:, None] * freq[None, :]).astype(np.float32)
    cos, sin = np.cos(ang.astype(np.float64)), np.sin(ang.astype(np.float64))
    cc = np.concatenate([cos, cos], 1).reshape(TB, P, 1, ROT)
    ss = np.concatenate([-sin, sin], 1).reshape(TB, P, 1, ROT)
    for at, tab in ((C_COS, cc), (C_SIN, ss)):
        full = np.broadcast_to(tab, (TB, P, 4, ROT)).transpose(1, 0, 2, 3)
        keep[:, at:at + TB * 4 * ROT] = full.reshape(P, -1).astype(np.float32)
    pool = np.zeros((P, C_POOL_END), np.float32)
    t = np.arange(SEQ)[:, None]
    s = np.arange(SEQ)[None, :]
    for g, w in enumerate(WINDOWS):
        count = np.minimum(np.arange(SEQ) + 1, w)
        band = ((t <= s) & (t > s - w)).astype(np.float32) - np.diag(count).astype(np.float32)
        pool[:, C_BAND + g * 384:C_BAND + g * 384 + 256] = band[:P]
        pool[:, C_BAND + g * 384 + 256:C_BAND + (g + 1) * 384] = band[P:, P:]
        pool[:, C_COUNT + g * SEQ:C_COUNT + (g + 1) * SEQ] = (np.float32(1) / count.astype(np.float32))[None]
    return keep, pool


def trunk(nc, x, mix_norm, mlp_norm, pool_w, pool_scale, kv_norm, w_kv, w_q, lam, subln, w_o,
          w_mlp_in, w_mlp_out, final_norm, keep_consts, pool_consts, out):
    with ExitStack() as ctx:
        def sb(name, shape, dt=F32, scope=ctx):
            return scope.enter_context(nc.sbuf_tensor(name, shape, dt))

        def sem(name):
            return ctx.enter_context(nc.semaphore(name))

        h = sb("h", [P, TB, D])
        keep = sb("keep", [P, C_END])
        gain = sb("gain", [P, G_ROWS])
        sub_gain = sb("sub_gain", [P, 2])
        ssq = sb("ssq", [P, 5, TB, NG])
        ssum = sb("ssum", [P, 5, TB])
        mean = sb("mean", [P, 5, TB])
        rms = sb("rms", [P, 5, TB])
        neg_half = sb("neg_half", [P, 4])
        lam_dots = sb("lam_dots", [P, 2])
        lam_exp = sb("lam_exp", [P, 2])
        lam_neg = sb("lam_neg", [P, 1])
        o_sq = sb("o_sq", [P, PAIRS, 4])
        o_mean = sb("o_mean", [P, PAIRS, 4])
        o_rms = sb("o_rms", [P, PAIRS, 4])
        row_max = sb("row_max", [P, PAIRS, 8])
        row_bias = sb("row_bias", [P, PAIRS, 8])
        row_sum = sb("row_sum", [P, PAIRS, 8])
        row_inv = sb("row_inv", [P, PAIRS, 8])
        row_lam = sb("row_lam", [P, PAIRS, 8])
        raw = sb("raw", [P, RAW, 2, SW])
        w_hi = sb("w_hi", [P, HALVES, 2, SW], F32R)
        w_lo = sb("w_lo", [P, HALVES, 2, SW], F32R)
        a_hi0 = sb("a_hi0", [P, 8, SEQ], F32R)
        a_lo0 = sb("a_lo0", [P, 8, SEQ], F32R)
        b_hi = sb("b_hi", [P, 16, SEQ], F32R)
        b_lo = sb("b_lo", [P, 16, SEQ], F32R)
        with ExitStack() as shared:
            a_hi1 = sb("a_hi1", [P, 8, SEQ], F32R, shared)
            a_lo1 = sb("a_lo1", [P, 8, SEQ], F32R, shared)
        q_t = sb("q_t", [P, 4, SEQ])
        probs = sb("probs", [P, 4, 384])
        attn_t = sb("attn_t", [P, 2, 384])
        lam_rows = sb("lam_rows", [P, 2, HD])
        lam_in = sb("lam_in", [P, 4, HD])
        scratch = sb("scratch", [P, 10752])

        def place(at, *shape):
            n = int(np.prod(shape))
            ap = scratch[:, at:at + n]
            if len(shape) == 2:
                ap = ap.rearrange("p (a b) -> p a b", b=shape[1])
            if len(shape) == 3:
                ap = ap.rearrange("p (a b c) -> p a b c", b=shape[1], c=shape[2])
            return ap
        x_norm = place(0, TB, D)
        pool_keep = place(4096, C_POOL_END)
        scale_row = place(4096 + C_POOL_END, D)
        scaled = place(4096 + C_POOL_END + D + 512, TB, SW)
        gain_rows = place(4096 + C_POOL_END + D + 512, P)
        relu = place(0, TB, SW)
        hidden = place(1024, TB, SW)
        junk = place(2048, TB, SW)
        final_row = place(3072, D)
        result = place(3072 + D, TB, D)
        k_t = place(0, 16, SEQ)
        v = place(4096, TB, D)
        kq = place(8192, TB, 4 * HD)
        rope_a = place(9216, TB, 4, ROT)
        rope_b = place(9472, TB, 4, ROT)
        o_n = place(9728, TB, SW)

        psum = [ctx.enter_context(nc.psum_tensor(f"bank{i}", [P, 512], F32)) for i in range(8)]
        X = psum[0:2]
        PAIR = (psum[2:4], psum[4:6])
        T = psum[6:8]

        x_landed = [sem(f"x_landed{tb}") for tb in range(TB)]
        x_squared = sem("x_squared")
        keep_landed = sem("keep_landed")
        pool_landed = sem("pool_landed")
        scale_landed = sem("scale_landed")
        gains_landed = sem("gains_landed")
        lam_landed = sem("lam_landed")
        final_landed = sem("final_landed")
        raw_landed = [sem(f"raw_landed{i}") for i in range(RAW)]
        hi_ready = sem("hi_ready")
        lo_ready = sem("lo_ready")
        pe_done = sem("pe_done")
        t_ready = sem("t_ready")
        t_hi = sem("t_hi")
        t_taken = sem("t_taken")
        h_added = sem("h_added")
        ssq_done = sem("ssq_done")
        sum_done = sem("sum_done")
        mean_done = sem("mean_done")
        rms_done = sem("rms_done")
        half_set = sem("half_set")
        gains_turned = sem("gains_turned")
        gains_ready = sem("gains_ready")
        x_normed = sem("x_normed")
        band_done = sem("band_done")
        pooled_done = sem("pooled_done")
        pooled_hi = sem("pooled_hi")
        pooled_lo = sem("pooled_lo")
        scaled_done = sem("scaled_done")
        relu_done = sem("relu_done")
        hidden_done = sem("hidden_done")
        kq_out = sem("kq_out")
        rope_parts = sem("rope_parts")
        rope_done = sem("rope_done")
        v_done = sem("v_done")
        lam_dot = sem("lam_dot")
        lam_exped = sem("lam_exped")
        lam_ready = sem("lam_ready")
        scores_done = sem("scores_done")
        max_done = sem("max_done")
        bias_done = sem("bias_done")
        exp_done = sem("exp_done")
        inv_done = sem("inv_done")
        lam_scaled = sem("lam_scaled")
        second_scaled = sem("second_scaled")
        diff_done = sem("diff_done")
        diff_turned = sem("diff_turned")
        attn_t_done = sem("attn_t_done")
        pv_done = sem("pv_done")
        o_sq_done = sem("o_sq_done")
        o_mean_done = sem("o_mean_done")
        o_rms_done = sem("o_rms_done")
        o_done = sem("o_done")
        gained = sem("gained")
        result_dve = sem("result_dve")
        result_act = sem("result_act")
        stored = sem("stored")

        def a_tile(kt):
            return (a_hi0[:, kt, :], a_lo0[:, kt, :]) if kt < 8 else (a_hi1[:, kt - 8, :], a_lo1[:, kt - 8, :])

        def b_tile(kt):
            return b_hi[:, kt, :], b_lo[:, kt, :]

        def by_block(ap):
            return ap.rearrange("p (b t) -> p b t", b=TB)

        def pooled(kt):
            return x_norm[:, :, kt * P:(kt + 1) * P]

        def o_tile(t, c):
            return a_tile(4 * t + c) if t < 2 else b_tile(4 * (t - 2) + c)

        U_FIRST, U_LAST = 8, 12

        block = ctx.enter_context(nc.Block())

        @block.sync
        def _(sp):
            def load_strip(s, source, first=False):
                for n in range(HALVES):
                    if not (first and n < RAW):
                        sp.wait_ge(lo_ready, s * HALVES + n - RAW + 1)
                    sp.dma_start(raw[:, n % RAW], source(n // 2, n % 2)).then_inc(raw_landed[n % RAW], 16)

            in_view = w_mlp_in.rearrange("l (c p) n -> l p c n", p=P)
            out_view = w_mlp_out.rearrange("l (c p) n -> l p c n", p=P)
            kv_view = w_kv.rearrange("(c p) n -> p c n", p=P)
            q_view = w_q.rearrange("l (c p) n -> l p c n", p=P)
            o_view = w_o.rearrange("l (c p) n -> l p c n", p=P)
            pool_view = pool_w.rearrange("l g (c p) n -> l g p c n", p=P)

            def in_rows(view, col):
                return lambda g, hf: view[:, 4 * g + 2 * hf:4 * g + 2 * hf + 2, bass.ds(col, SW)]

            def out_rows(view, j):
                return lambda g, hf: view[:, bass.ds(4 * j + 2 * hf, 2), SW * g:SW * (g + 1)]

            def load_mlp(layer):
                s0 = S_MLP[layer]
                load_strip(s0, in_rows(in_view[layer], 0))
                load_strip(s0 + 1, in_rows(in_view[layer], SW))
                with nc.sync.Fori(1, NJ - 1) as j:
                    load_strip(s0 + 2 * j, out_rows(out_view[layer], j - 1))
                    load_strip(s0 + 2 * j + 1, in_rows(in_view[layer], (j + 1) * SW))
                load_strip(s0 + 2 * NJ - 2, out_rows(out_view[layer], NJ - 2))
                load_strip(s0 + 2 * NJ - 1, out_rows(out_view[layer], NJ - 1))

            for tb in range(TB):
                sp.dma_start(h[:, tb, :], x[0, tb * P:(tb + 1) * P, :]).then_inc(x_landed[tb], 16)
            sp.dma_start(keep[:], keep_consts).then_inc(keep_landed, 16)
            sp.dma_start(pool_keep, pool_consts).then_inc(pool_landed, 16)
            load_strip(S_POOL, lambda g, hf: pool_view[0, g][:, 2 * hf:2 * hf + 2, :], first=True)
            load_mlp(0)
            with nc.sync.Fori(0, PAIRS) as j:
                load_strip(S_KV + 2 * j, in_rows(kv_view, j * SW))
                load_strip(S_KV + 2 * j + 1, in_rows(kv_view, j * SW + D))
            with nc.sync.Fori(0, PAIRS) as t:
                load_strip(S_Q + t, in_rows(q_view[0], t * SW))
            with nc.sync.Fori(0, PAIRS) as t:
                load_strip(S_O + t, out_rows(o_view[0], t))
            sp.wait_ge(o_done, 2 * PAIRS)
            sp.dma_start(final_row, final_norm.partition_broadcast(P)).then_inc(final_landed, 16)
            load_mlp(1)
            for i, (tb, cols) in enumerate(DVE_PIECES):
                sp.wait_ge(result_dve, i + 1)
                sp.dma_start(out[0, tb * P:(tb + 1) * P, cols], result[:, tb, cols]).then_inc(stored, 16)
            sp.wait_ge(stored, 16 * (len(DVE_PIECES) + len(ACT_PIECES)))

        @block.gpsimd
        def _(pool):
            nc.gpsimd.memset(neg_half[:], -0.5).then_inc(half_set, 1)
            pool.wait_ge(half_set, 1)

            def inv_rms(k):
                pool.wait_ge(mean_done, k + 1)
                nc.gpsimd.tensor_tensor(rms[:, k, :], mean[:, k, :], neg_half[:, 0:TB], ALU.pow).then_inc(rms_done, 1)

            for k in range(3):
                inv_rms(k)
            for t in range(PAIRS):
                pool.wait_ge(o_mean_done, t + 1)
                nc.gpsimd.tensor_tensor(o_rms[:, t, :], o_mean[:, t, :], neg_half[:], ALU.pow).then_inc(o_rms_done, 1)
            for k in range(3, 5):
                inv_rms(k)

        @block.scalar
        def _(act):
            def split(s, g, first=False):
                for n in (2 * g, 2 * g + 1):
                    act.wait_ge(raw_landed[n % RAW], 16 * (2 * s + n // RAW + 1))
                    if not first:
                        act.wait_ge(pe_done, (s - 1) * HALVES + n + 1)
                    nc.scalar.activation(w_hi[:, n], raw[:, n % RAW], ACT.Copy).then_inc(hi_ready, 1)

            def h_squares(k, n, count):
                act.wait_ge(h_added, count)
                for tb in range(TB):
                    done = 1 + (k - 1) * TB * NG + n * TB + tb
                    if n > 0:
                        act.wait_ge(ssq_done, done - 1)
                    nc.scalar.activation(junk[:, tb] if k > 1 else x_norm[:, tb, n * SW:(n + 1) * SW],
                                         h[:, tb, n * SW:(n + 1) * SW], ACT.Square,
                                         accum_out=ssq[:, k, tb, n:n + 1]).then_inc(ssq_done, 1)

            def h_hi(k, n):
                if k == 0 and n == 0:
                    act.wait_ge(gains_ready, 1)
                for b in range(2):
                    act.wait_ge(t_ready, 2 * (R_H[k] + n) + b + 1)
                    for c in (2 * b, 2 * b + 1):
                        src = T[b][:, (c % 2) * SEQ:(c % 2 + 1) * SEQ]
                        kt = 4 * n + c
                        if k == 1:
                            nc.scalar.activation(b_tile(kt)[0], src, ACT.Copy, scale=gain[:, G_MIX + 16 + kt:G_MIX + 17 + kt])
                            col = G_KV + kt
                        else:
                            col = G_MLP + (16 if k == 2 else 0) + kt
                        last = nc.scalar.activation(a_tile(kt)[0], src, ACT.Copy, scale=gain[:, col:col + 1])
                    last.then_inc(t_hi, 1)

            def u_hi(j, layer, at):
                for b in range(2):
                    act.wait_ge(t_ready, 2 * (j + R_U[layer]) + b + 1)
                    nc.scalar.activation(b_hi[:, at + 2 * b:at + 2 * b + 2, :], T[b][:].rearrange("p (c t) -> p c t", c=2),
                                         ACT.Copy).then_inc(t_hi, 1)

            def u_relu(j, layer, s, banks):
                act.wait_ge(pe_done, s * HALVES + HALVES)
                for tb in range(TB):
                    nc.scalar.activation(relu[:, tb], banks[tb][:], ACT.Relu,
                                         scale=rms[:, 2 * layer + 1, tb:tb + 1]).then_inc(relu_done, 1)

            def mlp(layer):
                s0, k = S_MLP[layer], 2 * layer
                for g in range(NG):
                    if g == 3:
                        act.wait_ge(rms_done, k + 2)
                        u_relu(0, layer, s0, PAIR[0])
                    split(s0 + 1, g)
                    if g < 2:
                        h_hi(k, g + 2)
                for g in range(NG):
                    if g == 3:
                        act.wait_ge(hidden_done, TB * (NJ * layer + 1))
                        u_relu(1, layer, s0 + 1, X)
                    split(s0 + 2, g)
                    if g == 1:
                        u_hi(0, layer, U_FIRST)
                with nc.scalar.Fori(1, NJ - 1) as j:
                    for g in range(NG):
                        split(s0 + 2 * j + 1, g)
                    for g in range(NG):
                        if g == 3:
                            act.wait_ge(hidden_done, (j + NJ * layer + 1) * TB)
                            u_relu(j + 1, layer, s0 + 2 * j + 1, X)
                        split(s0 + 2 * j + 2, g)
                        if g == 1:
                            u_hi(j, layer, U_FIRST)
                for g in range(NG):
                    split(s0 + 2 * NJ - 1, g)
                    if g == 1:
                        u_hi(NJ - 1, layer, U_LAST)
                for g in range(NG):
                    if layer == 0:
                        split(s0 + 2 * NJ, g)
                    h_squares(k + 2, g, H_MLP[layer] + NG * (NJ - 1) + g + 1)
                    if layer == 0 and g >= 2:
                        h_hi(1, g - 2)

            act.dma_start(gain_rows[G_MIX:G_MIX + 32, :], mix_norm.rearrange("l (k p) -> (l k) p", p=P)).then_inc(gains_landed, 16)
            act.dma_start(gain_rows[G_MLP:G_MLP + 32, :], mlp_norm.rearrange("l (k p) -> (l k) p", p=P)).then_inc(gains_landed, 16)
            act.dma_start(gain_rows[G_KV:G_KV + 16, :], kv_norm.rearrange("(k p) -> k p", p=P)).then_inc(gains_landed, 16)
            act.dma_start(gain_rows[G_SUB:G_SUB + 2, :], subln.rearrange("l (k p) -> (l k) p", p=P)).then_inc(gains_landed, 16)
            act.wait_ge(x_landed[0], 16)
            nc.scalar.activation(x_norm[:, 0, :], h[:, 0, :], ACT.Square, accum_out=ssq[:, 0, 0, 0:1]).then_inc(ssq_done, 1)
            act.dma_start(scale_row, pool_scale.rearrange("l d -> (l d)").partition_broadcast(P)).then_inc(scale_landed, 16)

            act.wait_ge(rms_done, 1)
            for n in range(NG):
                for tb in range(TB):
                    cols = slice(n * SW, (n + 1) * SW)
                    nc.scalar.activation(x_norm[:, tb, cols], h[:, tb, cols], ACT.Copy,
                                         scale=rms[:, 0, tb:tb + 1]).then_inc(x_normed, 1)
                if n == 1:
                    split(0, 0, first=True)

            def pooled_to_hi(n):
                for c in range(4):
                    act.wait_ge(pooled_done, 4 * n + c + 1)
                    nc.scalar.activation(by_block(b_tile(4 * n + c)[0]), pooled(4 * n + c), ACT.Copy).then_inc(pooled_hi, 1)
            pooled_to_hi(0)
            split(0, 1, first=True)
            pooled_to_hi(1)
            split(0, 2, first=True)
            split(0, 3, first=True)
            for g in range(NG):
                if g + 2 < NG:
                    pooled_to_hi(g + 2)
                split(1, g)
                h_squares(1, g, H_POOL + g + 1)
                if g >= 2:
                    h_hi(0, g - 2)

            mlp(0)

            def kq_copy(i, s, r):
                act.wait_ge(pe_done, s * HALVES + HALVES)
                act.wait_ge(t_ready, r)
                for tb in range(TB):
                    nc.scalar.activation(kq[:, tb], PAIR[i][tb][:], ACT.Copy, scale=rms[:, 2, tb:tb + 1]).then_inc(kq_out, 1)

            for g in range(NG):
                if g == 3:
                    act.wait_ge(rms_done, 3)
                    kq_copy(0, S_KV, 2 * R_K)
                split(S_KV + 1, g)
                if g < 2:
                    h_hi(1, g + 2)
            for g in range(NG):
                split(S_KV + 2, g)
            with nc.scalar.Fori(1, PAIRS) as j:
                for g in range(NG):
                    if g == 3:
                        kq_copy(0, S_KV + 2 * j, (j + R_K) * 2)
                    split(S_KV + 2 * j + 1, g)
                for g in range(NG):
                    split(S_KV + 2 * j + 2, g)

            def exps(t, hcs):
                for hc in hcs:
                    act.wait_ge(bias_done, 2 * t + hc // 2 + 1)
                    for qb in range(2):
                        cols = slice(0, 128) if qb == 0 else slice(128, 384)
                        nc.scalar.activation(probs[:, hc, cols], probs[:, hc, cols], ACT.Exp,
                                             bias=row_bias[:, t, 2 * hc + qb:2 * hc + qb + 1], scale=SM_SCALE,
                                             accum_out=row_sum[:, t, 2 * hc + qb:2 * hc + qb + 1]).then_inc(exp_done, 1)

            for t in range(2 * PAIRS):
                s = S_Q + t
                for g in range(NG):
                    if g == 3 and t < PAIRS:
                        kq_copy(t % 2, s, 2 * (R_ATT[("q", t - 1)] + 1) if t else 2 * (R_K + PAIRS))
                    split(s + 1, g)
                    if t == 2 * PAIRS - 1:
                        h_squares(3, g, H_O + NG * t - NG * PAIRS + g + 1)
                    if t == 0 and g == 0:
                        act.wait_ge(pe_done, S_Q * HALVES)
                        act.dma_start(lam_in[:].rearrange("p a b -> p (a b)"),
                                      lam.rearrange("l a b -> (l a b)").partition_broadcast(P)).then_inc(lam_landed, 16)
                    if t == 0 and g == 2:
                        act.wait_ge(lam_dot, 2)
                        nc.scalar.activation(lam_exp[:], lam_dots[:], ACT.Exp).then_inc(lam_exped, 1)
                    if g == 3 and 0 <= t - 2 < PAIRS:
                        for hh in range(2):
                            act.wait_ge(pv_done, 2 * (t - 2) + hh + 1)
                            for tb in range(TB):
                                nc.scalar.activation(o_n[:, tb, hh * VD:(hh + 1) * VD], X[hh][:, tb * VD:(tb + 1) * VD], ACT.Square,
                                                     accum_out=o_sq[:, t - 2, 2 * hh + tb:2 * hh + tb + 1]).then_inc(o_sq_done, 1)
                    if g == 1 and 0 <= t - 3 < PAIRS:
                        for b in range(2):
                            act.wait_ge(t_ready, 2 * R_ATT[("o", t - 3)] + b + 1)
                            for c in (2 * b, 2 * b + 1):
                                last = nc.scalar.activation(o_tile(t - 3, c)[0], T[b][:, (c % 2) * SEQ:(c % 2 + 1) * SEQ],
                                                            ACT.Copy, scale=sub_gain[:, c % 2:c % 2 + 1])
                            last.then_inc(t_hi, 1)
                    if g == 1 and 0 <= t - 1 < PAIRS:
                        exps(t - 1, (0, 1))
                    if g == 2 and 0 <= t - 1 < PAIRS:
                        exps(t - 1, (2, 3))
                    if t == 2 * PAIRS - 1 and g >= 2:
                        h_hi(2, g - 2)

            mlp(1)

            act.wait_ge(rms_done, 5)
            act.wait_ge(gained, NG)
            for i, (tb, cols) in enumerate(ACT_PIECES):
                nc.scalar.activation(result[:, tb, cols], result[:, tb, cols], ACT.Copy, scale=rms[:, 4, tb:tb + 1]).then_inc(result_act, 1)
                act.wait_ge(result_act, i + 1)
                act.dma_start(out[0, tb * P:(tb + 1) * P, cols], result[:, tb, cols]).then_inc(stored, 16)

        @block.vector
        def _(dve):
            def split(s, g):
                for n in (2 * g, 2 * g + 1):
                    dve.wait_ge(hi_ready, s * HALVES + n + 1)
                    nc.vector.tensor_tensor(w_lo[:, n], raw[:, n % RAW], w_hi[:, n].bitcast(F32), ALU.subtract).then_inc(lo_ready, 1)

            def norm_mean(k):
                dve.wait_ge(ssq_done, 1 + k * TB * NG)
                if k:
                    nc.vector.tensor_reduce(ssum[:, k, :], ssq[:, k], AX.X, ALU.add).then_inc(sum_done, 1)
                    dve.wait_ge(sum_done, k)
                src = ssum[:, k, :] if k else ssq[:, 0, :, 0]
                nc.vector.tensor_scalar(mean[:, k, :], src, 1.0 / D, EPS, ALU.mult, ALU.add).then_inc(mean_done, 1)

            def h_lo(k, n):
                for b in range(2):
                    dve.wait_ge(t_hi, 2 * (X_H[k] + n) + b + 1)
                    for c in (2 * b, 2 * b + 1):
                        src = T[b][:, (c % 2) * SEQ:(c % 2 + 1) * SEQ]
                        kt = 4 * n + c
                        if k == 1:
                            hi, lo = b_tile(kt)
                            nc.vector.scalar_tensor_tensor(lo, src, gain[:, G_MIX + 16 + kt:G_MIX + 17 + kt], hi.bitcast(F32),
                                                           ALU.mult, ALU.subtract)
                            col = G_KV + kt
                        else:
                            col = G_MLP + (16 if k == 2 else 0) + kt
                        hi, lo = a_tile(kt)
                        last = nc.vector.scalar_tensor_tensor(lo, src, gain[:, col:col + 1], hi.bitcast(F32), ALU.mult, ALU.subtract)
                    last.then_inc(t_taken, 1)

            def u_lo(j, layer, at):
                for b in range(2):
                    dve.wait_ge(t_hi, 2 * (j + X_U[layer]) + b + 1)
                    tiles = slice(at + 2 * b, at + 2 * b + 2)
                    nc.vector.tensor_tensor(b_lo[:, tiles, :], T[b][:].rearrange("p (c t) -> p c t", c=2),
                                            b_hi[:, tiles, :].bitcast(F32), ALU.subtract).then_inc(t_taken, 1)

            def u_square(j, layer, banks):
                for tb in range(TB):
                    dve.wait_ge(relu_done, (j + NJ * layer) * TB + tb + 1)
                    nc.vector.scalar_tensor_tensor(hidden[:, tb], banks[tb][:], rms[:, 2 * layer + 1, tb:tb + 1], relu[:, tb],
                                                   ALU.mult, ALU.mult).then_inc(hidden_done, 1)

            def h_add(s, g):
                dve.wait_ge(pe_done, s * HALVES + 2 * g + 2)
                cols = slice(g * SW, (g + 1) * SW)
                for tb in range(TB):
                    last = nc.vector.tensor_tensor(h[:, tb, cols], PAIR[g % 2][tb][:], h[:, tb, cols], ALU.add)
                last.then_inc(h_added, 1)

            def mlp(layer):
                s0, k = S_MLP[layer], 2 * layer
                for g in range(NG):
                    if g == 3:
                        dve.wait_ge(rms_done, k + 2)
                        u_square(0, layer, PAIR[0])
                    split(s0 + 1, g)
                    if g < 2:
                        h_lo(k, g + 2)
                for g in range(NG):
                    if g == 3:
                        u_square(1, layer, X)
                    split(s0 + 2, g)
                    if g == 1:
                        u_lo(0, layer, U_FIRST)
                with nc.vector.Fori(1, NJ - 1) as j:
                    for g in range(NG):
                        h_add(s0 + 2 * j, g)
                        split(s0 + 2 * j + 1, g)
                    for g in range(NG):
                        if g == 3:
                            u_square(j + 1, layer, X)
                        split(s0 + 2 * j + 2, g)
                        if g == 1:
                            u_lo(j, layer, U_FIRST)
                for g in range(NG):
                    h_add(s0 + 2 * NJ - 2, g)
                    split(s0 + 2 * NJ - 1, g)
                    if g == 1:
                        u_lo(NJ - 1, layer, U_LAST)
                for g in range(NG):
                    h_add(s0 + 2 * NJ - 1, g)
                    if layer == 1:
                        cols = slice(g * SW, (g + 1) * SW)
                        dve.wait_ge(final_landed, 16)
                        dve.wait_ge(h_added, H_MLP[1] + NG * (NJ - 1) + g + 1)
                        for tb in range(TB):
                            last = nc.vector.tensor_tensor(result[:, tb, cols], h[:, tb, cols], final_row[:, cols], ALU.mult)
                        last.then_inc(gained, 1)
                    if s0 + 2 * NJ < STRIPS:
                        split(s0 + 2 * NJ, g)
                        if g >= 2:
                            h_lo(1, g - 2)

            dve.wait_ge(x_landed[1], 16)
            nc.vector.tensor_tensor_reduce(x_norm[:, 1, :], h[:, 1, :], h[:, 1, :], 1.0, 0.0, ALU.mult, ALU.add,
                                           ssq[:, 0, 1, 0:1]).then_inc(x_squared, 1)
            dve.wait_ge(x_squared, 1)
            norm_mean(0)
            dve.wait_ge(gains_turned, 1)
            nc.vector.tensor_copy(gain[:], X[0][:, 0:G_ROWS]).then_inc(gains_ready, 1)
            dve.wait_ge(gains_ready, 1)
            nc.vector.tensor_scalar(sub_gain[:], gain[:, G_SUB:G_SUB + 2], 1.0 - LAM_INIT, None, ALU.mult).then_inc(gains_ready, 1)
            dve.wait_ge(pool_landed, 16)

            def pooled_parts(n):
                for c in range(4):
                    kt = 4 * n + c
                    dve.wait_ge(band_done, 2 * n + c // 2 + 1)
                    nc.vector.scalar_tensor_tensor(pooled(kt), by_block(T[c // 2][:, (c % 2) * SEQ:(c % 2 + 1) * SEQ]),
                                                   gain[:, G_MIX + kt:G_MIX + kt + 1],
                                                   by_block(pool_keep[:, C_COUNT + n * SEQ:C_COUNT + (n + 1) * SEQ]),
                                                   ALU.mult, ALU.mult).then_inc(pooled_done, 1)
                for c in range(4):
                    kt = 4 * n + c
                    dve.wait_ge(pooled_hi, kt + 1)
                    hi, lo = b_tile(kt)
                    nc.vector.tensor_tensor(by_block(lo), pooled(kt), by_block(hi.bitcast(F32)), ALU.subtract).then_inc(pooled_lo, 1)

            split(0, 0)
            pooled_parts(0)
            split(0, 1)
            pooled_parts(1)
            split(0, 2)
            split(0, 3)
            dve.wait_ge(scale_landed, 16)
            for g in range(NG):
                if g + 2 < NG:
                    pooled_parts(g + 2)
                dve.wait_ge(pe_done, 2 * g + 2)
                if g:
                    dve.wait_ge(h_added, g)
                cols = slice(g * SW, (g + 1) * SW)
                for tb in range(TB):
                    nc.vector.tensor_tensor(scaled[:, tb], PAIR[g % 2][tb][:], scale_row[:, cols], ALU.mult).then_inc(scaled_done, 1)
                for tb in range(TB):
                    dve.wait_ge(scaled_done, TB * g + tb + 1)
                    last = nc.vector.tensor_tensor(h[:, tb, cols], scaled[:, tb], h[:, tb, cols], ALU.add)
                last.then_inc(h_added, 1)
                split(1, g)
                if g >= 2:
                    h_lo(0, g - 2)
            norm_mean(1)

            mlp(0)
            norm_mean(2)

            def rope(i):
                dve.wait_ge(kq_out, (i + 1) * TB)
                heads = kq.rearrange("p b (c d) -> p b c d", d=HD)
                cos = keep[:, C_COS:C_COS + TB * 4 * ROT].rearrange("p (b c d) -> p b c d", b=TB, d=ROT)
                sin = keep[:, C_SIN:C_SIN + TB * 4 * ROT].rearrange("p (b c d) -> p b c d", b=TB, d=ROT)
                hr = ROT // 2
                nc.vector.tensor_tensor(rope_a, heads[:, :, :, 0:ROT], cos, ALU.mult).then_inc(rope_parts, 1)
                nc.vector.tensor_tensor(rope_b[:, :, :, 0:hr], heads[:, :, :, hr:ROT], sin[:, :, :, 0:hr], ALU.mult).then_inc(rope_parts, 1)
                nc.vector.tensor_tensor(rope_b[:, :, :, hr:ROT], heads[:, :, :, 0:hr], sin[:, :, :, hr:ROT], ALU.mult).then_inc(rope_parts, 1)
                dve.wait_ge(rope_parts, (i + 1) * 3)
                nc.vector.tensor_tensor(heads[:, :, :, 0:ROT], rope_a, rope_b, ALU.add).then_inc(rope_done, 1)

            def v_out(j):
                dve.wait_ge(pe_done, (j * 2 + S_KV + 2) * HALVES)
                for tb in range(TB):
                    last = nc.vector.tensor_scalar(v[:, tb, bass.ds(j * SW, SW)], PAIR[1][tb][:], rms[:, 2, tb:tb + 1], None, ALU.mult)
                last.then_inc(v_done, 1)

            def k_turned(j):
                for b in range(2):
                    dve.wait_ge(t_ready, 2 * (j + R_K) + b + 1)
                    nc.vector.tensor_copy(k_t[:, bass.ds(j * 4 + 2 * b, 2), :], T[b][:].rearrange("p (c t) -> p c t", c=2)).then_inc(t_taken, 1)

            for g in range(NG):
                if g == 3:
                    dve.wait_ge(rms_done, 3)
                    rope(0)
                split(S_KV + 1, g)
                if g < 2:
                    h_lo(1, g + 2)
            for g in range(NG):
                if g == 3:
                    v_out(0)
                split(S_KV + 2, g)
                if g == 1:
                    k_turned(0)
            with nc.vector.Fori(1, PAIRS) as j:
                for g in range(NG):
                    if g == 3:
                        rope(j)
                    split(S_KV + 2 * j + 1, g)
                for g in range(NG):
                    if g == 3:
                        v_out(j)
                    split(S_KV + 2 * j + 2, g)
                    if g == 1:
                        k_turned(j)

            QB = (slice(0, 128), slice(128, 384))

            def negative_lambda():
                dve.wait_ge(lam_landed, 16)
                for i in range(2):
                    nc.vector.tensor_tensor_reduce(lam_rows[:, i, :], lam_in[:, 2 * i, :], lam_in[:, 2 * i + 1, :], 1.0, 0.0,
                                                   ALU.mult, ALU.add, lam_dots[:, i:i + 1]).then_inc(lam_dot, 1)
                dve.wait_ge(lam_exped, 1)
                nc.vector.scalar_tensor_tensor(lam_neg[:], lam_exp[:, 1:2], -LAM_INIT, lam_exp[:, 0:1], ALU.add, ALU.subtract).then_inc(lam_ready, 1)

            def maxima(t, half):
                for hc in (2 * half, 2 * half + 1):
                    dve.wait_ge(scores_done, 4 * t + hc + 1)
                    for qb in range(2):
                        nc.vector.tensor_tensor_reduce(probs[:, hc, QB[qb]], X[hc % 2][:, QB[qb]],
                                                       keep[:, C_MASK + QB[qb].start:C_MASK + QB[qb].stop], 1.0, -3.4e38,
                                                       ALU.add, ALU.max, row_max[:, t, 2 * hc + qb:2 * hc + qb + 1]).then_inc(max_done, 1)
                dve.wait_ge(max_done, 8 * t + 4 * half + 4)
                nc.vector.tensor_scalar(row_bias[:, t, 4 * half:4 * half + 4], row_max[:, t, 4 * half:4 * half + 4],
                                        -SM_SCALE, None, ALU.mult).then_inc(bias_done, 1)

            def differences(t):
                dve.wait_ge(exp_done, 8 * (t + 1))
                nc.vector.reciprocal(row_inv[:, t, :], row_sum[:, t, :]).then_inc(inv_done, 1)
                dve.wait_ge(inv_done, t + 1)
                if t == 0:
                    dve.wait_ge(lam_ready, 1)
                nc.vector.tensor_scalar(row_lam[:, t, :], row_inv[:, t, :], lam_neg[:, 0:1], None, ALU.mult).then_inc(lam_scaled, 1)
                dve.wait_ge(lam_scaled, t + 1)
                for hh in range(2):
                    for qb in range(2):
                        at = 4 * hh + 2 + qb
                        nc.vector.tensor_scalar(probs[:, 2 * hh + 1, QB[qb]], probs[:, 2 * hh + 1, QB[qb]],
                                                row_lam[:, t, at:at + 1], None, ALU.mult).then_inc(second_scaled, 1)
                for hh in range(2):
                    for qb in range(2):
                        at = 4 * hh + qb
                        dve.wait_ge(second_scaled, 4 * t + 2 * hh + qb + 1)
                        nc.vector.scalar_tensor_tensor(probs[:, 2 * hh, QB[qb]], probs[:, 2 * hh, QB[qb]], row_inv[:, t, at:at + 1],
                                                       probs[:, 2 * hh + 1, QB[qb]], ALU.mult, ALU.add).then_inc(diff_done, 1)

            for t in range(2 * PAIRS):
                s = S_Q + t
                for g in range(NG):
                    if t >= PAIRS:
                        h_add(s, g)
                    if g == 3 and t < PAIRS:
                        rope(PAIRS + t)
                    split(s + 1, g)
                    if t == 0 and g == 2:
                        negative_lambda()
                    if g == 0 and 0 <= t - 1 < PAIRS:
                        for b in range(2):
                            dve.wait_ge(t_ready, 2 * R_ATT[("q", t - 1)] + b + 1)
                            nc.vector.tensor_copy(q_t[:, 2 * b:2 * b + 2, :], T[b][:].rearrange("p (c t) -> p c t", c=2)).then_inc(t_taken, 1)
                    if g == 1 and 0 <= t - 3 < PAIRS:
                        for b in range(2):
                            dve.wait_ge(t_hi, 2 * (X_O + t - 3) + b + 1)
                            for c in (2 * b, 2 * b + 1):
                                hi, lo = o_tile(t - 3, c)
                                last = nc.vector.scalar_tensor_tensor(lo, T[b][:, (c % 2) * SEQ:(c % 2 + 1) * SEQ], sub_gain[:, c % 2:c % 2 + 1],
                                                                      hi.bitcast(F32), ALU.mult, ALU.subtract)
                            last.then_inc(t_taken, 1)
                    if g == 0 and 0 <= t - 2 < PAIRS:
                        for hh in range(2):
                            dve.wait_ge(diff_turned, 2 * (t - 2) + hh + 1)
                            nc.vector.tensor_copy(attn_t[:, hh, :], X[hh][:, 0:384]).then_inc(attn_t_done, 1)
                    if g in (1, 2) and 0 <= t - 1 < PAIRS:
                        maxima(t - 1, g - 1)
                    if g == 2 and 0 <= t - 1 < PAIRS:
                        differences(t - 1)
                    if g == 3 and 0 <= t - 2 < PAIRS:
                        dve.wait_ge(o_sq_done, 4 * (t - 1))
                        nc.vector.tensor_scalar(o_mean[:, t - 2, :], o_sq[:, t - 2, :], 1.0 / VD, EPS, ALU.mult, ALU.add).then_inc(o_mean_done, 1)
                        dve.wait_ge(o_rms_done, t - 1)
                        for hh in range(2):
                            for tb in range(TB):
                                last = nc.vector.tensor_scalar(o_n[:, tb, hh * VD:(hh + 1) * VD], X[hh][:, tb * VD:(tb + 1) * VD],
                                                               o_rms[:, t - 2, 2 * hh + tb:2 * hh + tb + 1], None, ALU.mult)
                            last.then_inc(o_done, 1)
                    if t == 2 * PAIRS - 1 and g >= 2:
                        h_lo(2, g - 2)
            norm_mean(3)

            mlp(1)

            norm_mean(4)
            dve.wait_ge(rms_done, 5)
            dve.wait_ge(gained, NG)
            for tb, cols in DVE_PIECES:
                nc.vector.tensor_scalar(result[:, tb, cols], result[:, tb, cols], rms[:, 4, tb:tb + 1], None, ALU.mult).then_inc(result_dve, 1)

        @block.tensor
        def _(pe):
            ident = keep[:, C_IDENT:C_IDENT + P]

            def group(s, g, tiles, banks, start, stop):
                for hf in range(2):
                    n = 2 * g + hf
                    pe.wait_ge(lo_ready, s * HALVES + n + 1)
                    for kk in range(2):
                        hi, lo = tiles[2 * hf + kk]
                        begin = start and hf == 0 and kk == 0
                        end = stop and hf == 1 and kk == 1
                        for tb in range(TB):
                            tok = slice(tb * P, (tb + 1) * P)
                            nc.tensor.matmul(banks[tb][:], hi[:, tok], w_hi[:, n, kk, :], start=begin, stop=False)
                            nc.tensor.matmul(banks[tb][:], hi[:, tok], w_lo[:, n, kk, :], start=False, stop=False)
                            last = nc.tensor.matmul(banks[tb][:], lo[:, tok], w_hi[:, n, kk, :], start=False, stop=end)
                    last.then_inc(pe_done, 1)

            def in_group(s, g, tile, banks):
                group(s, g, [tile(4 * g + c) for c in range(4)], banks, g == 0, g == 3)

            def turn(r, source, first=False):
                for b in range(2):
                    if first:
                        pe.wait_ge(pooled_done, 4 * NG - 2 + 2 * b)
                    else:
                        pe.wait_ge(t_taken, (r - 1) * 2 + b + 1)
                    for c in (2 * b, 2 * b + 1):
                        for tb in range(TB):
                            at = (c % 2) * SEQ + tb * P
                            last = nc.tensor.transpose(T[b][:, at:at + P], source(tb, c), ident)
                    last.then_inc(t_ready, 1)

            def turn_h(k, n, count):
                pe.wait_ge(h_added, count)
                turn(R_H[k] + n, lambda tb, c: h[:, tb, n * SW + c * P:n * SW + (c + 1) * P], first=(k == 0 and n == 0))

            def turn_u(j, layer):
                pe.wait_ge(hidden_done, (j + NJ * layer + 1) * TB)
                turn(j + R_U[layer], lambda tb, c: hidden[:, tb, c * P:(c + 1) * P])

            def out_strip(s, at, layer, j, hooks):
                pe.wait_ge(t_taken, (j + R_U[layer]) * 2 + 2)
                for g in range(NG):
                    pe.wait_ge(h_added, j * NG + (H_MLP[layer] + g - 1))
                    group(s, g, [b_tile(at + c) for c in range(4)], PAIR[g % 2], True, True)
                    hooks(g)

            def mlp(layer):
                s0, k, h0 = S_MLP[layer], 2 * layer, H_MLP[layer]
                pe.wait_ge(h_added, h0 - 1)
                for g in range(NG):
                    pe.wait_ge(t_taken, 2 * (R_H[k] + g) + 2)
                    in_group(s0, g, a_tile, PAIR[0])
                    if g < 2:
                        turn_h(k, g + 2, h0 - NG + g + 3)
                if layer == 0:
                    pe.wait_ge(gains_ready, 1)
                else:
                    pe.wait_ge(o_done, 2 * PAIRS)
                for g in range(NG):
                    in_group(s0 + 1, g, a_tile, X)
                    if g == 1:
                        turn_u(0, layer)
                with nc.tensor.Fori(1, NJ - 1) as j:
                    out_strip(s0 + 2 * j, U_FIRST, layer, j - 1, lambda g: None)
                    pe.wait_ge(hidden_done, (j + NJ * layer + 1) * TB)
                    for g in range(NG):
                        in_group(s0 + 2 * j + 1, g, a_tile, X)
                        if g == 1:
                            turn_u(j, layer)
                out_strip(s0 + 2 * NJ - 2, U_FIRST, layer, NJ - 2, lambda g: turn_u(NJ - 1, layer) if g == 1 else None)
                done = h0 + NG * (NJ - 1)
                out_strip(s0 + 2 * NJ - 1, U_LAST, layer, NJ - 1,
                          lambda g: turn_h(1, g - 2, done + g - 1) if g >= 2 and layer == 0 else None)

            pe.wait_ge(keep_landed, 16)
            pe.wait_ge(gains_landed, 64)
            nc.tensor.transpose(X[0][:, 0:G_ROWS], gain_rows[0:G_ROWS, :], ident[0:G_ROWS, 0:G_ROWS]).then_inc(gains_turned, 1)

            def bands(n):
                pe.wait_ge(x_normed, TB * (n + 1))
                for b in range(2):
                    if n:
                        pe.wait_ge(pooled_done, 4 * n - 2 + 2 * b)
                    for c in (2 * b, 2 * b + 1):
                        cols = slice((4 * n + c) * P, (4 * n + c + 1) * P)
                        at = (c % 2) * SEQ
                        band = C_BAND + n * 384
                        nc.tensor.matmul(T[b][:, at:at + REACH], x_norm[:, 0, cols], pool_keep[:, band:band + REACH],
                                         start=True, stop=False, skip_group_check=True)
                        last = nc.tensor.matmul(T[b][:, at + P:at + SEQ], x_norm[:, 1, cols], pool_keep[:, band + 256:band + 384],
                                                start=False, stop=True, skip_group_check=True)
                    last.then_inc(band_done, 1)

            pe.wait_ge(pool_landed, 16)
            bands(0)
            bands(1)
            for g in range(NG):
                pe.wait_ge(pooled_lo, 4 * (g + 1))
                if g >= 2:
                    pe.wait_ge(h_added, g - 1)
                group(S_POOL, g, [b_tile(4 * g + c) for c in range(4)], PAIR[g % 2], True, True)
                if g + 2 < NG:
                    bands(g + 2)
                else:
                    turn_h(0, g - 2, g - 1)

            mlp(0)

            kq4 = lambda tb, c: kq[:, tb, c * HD:(c + 1) * HD]

            def kv_pair(j, first):
                if first:
                    pe.wait_ge(h_added, H_O - 1)
                else:
                    pe.wait_ge(kq_out, j * TB)
                for g in range(NG):
                    if first:
                        pe.wait_ge(t_taken, 2 * (R_H[1] + g) + 2)
                    in_group(S_KV + 2 * j, g, a_tile, PAIR[0])
                    if first and g < 2:
                        turn_h(1, g + 2, H_O - NG + g + 3)
                if first:
                    pe.wait_ge(h_added, H_O)
                else:
                    pe.wait_ge(v_done, j)
                for g in range(NG):
                    in_group(S_KV + 2 * j + 1, g, a_tile, PAIR[1])
                    if g == 1:
                        pe.wait_ge(rope_done, j + 1)
                        turn(j + R_K, kq4)

            kv_pair(0, True)
            with nc.tensor.Fori(1, PAIRS) as j:
                kv_pair(j, False)

            def scores(t, hc):
                k = k_t[:, 4 * t + hc, :]
                nc.tensor.matmul(X[hc % 2][:, 0:128], q_t[:, hc, 0:P], k[:, 0:P], start=True, stop=True)
                nc.tensor.matmul(X[hc % 2][:, 128:384], q_t[:, hc, P:SEQ], k, start=True, stop=True).then_inc(scores_done, 1)

            def attention(t, g):
                if g == 0 and 0 <= t - 1 < PAIRS:
                    pe.wait_ge(rope_done, PAIRS + t)
                    turn(R_ATT[("q", t - 1)], kq4)
                if g == 0 and 0 <= t - 2 < PAIRS:
                    u = t - 2
                    pe.wait_ge(diff_done, 4 * (u + 1))
                    if u:
                        pe.wait_ge(o_done, 2 * u)
                    else:
                        pe.wait_ge(max_done, 8 * (u + 1))
                    for hh in range(2):
                        for i in range(3):
                            cols = slice(i * P, (i + 1) * P)
                            last = nc.tensor.transpose(X[hh][:, cols], probs[:, 2 * hh, cols], ident)
                        last.then_inc(diff_turned, 1)
                if g in (1, 2) and 0 <= t - 1 < PAIRS:
                    u = t - 1
                    if g == 1:
                        pe.wait_ge(t_taken, 2 * R_ATT[("q", u)] + 2)
                        if u:
                            pe.wait_ge(attn_t_done, 2 * u)
                        else:
                            pe.wait_ge(hidden_done, TB * NJ)
                    else:
                        pe.wait_ge(max_done, 8 * u + 4)
                    scores(u, 2 * g - 2)
                    scores(u, 2 * g - 1)
                if g == 1 and 0 <= t - 3 < PAIRS:
                    pe.wait_ge(o_done, 2 * (t - 2))
                    turn(R_ATT[("o", t - 3)], lambda tb, c: o_n[:, tb, c * P:(c + 1) * P])
                if g == 3 and 0 <= t - 2 < PAIRS:
                    u = t - 2
                    pe.wait_ge(attn_t_done, 2 * (u + 1))
                    pe.wait_ge(max_done, 8 * min(u + 2, PAIRS))
                    for hh in range(2):
                        cols = slice((2 * u + hh) * VD, (2 * u + hh + 1) * VD)
                        nc.tensor.matmul(X[hh][:, 0:VD], attn_t[:, hh, 0:P], v[:, 0, cols], start=True, stop=True)
                        nc.tensor.matmul(X[hh][:, VD:2 * VD], attn_t[:, hh, P:2 * P], v[:, 0, cols], start=True, stop=False)
                        nc.tensor.matmul(X[hh][:, VD:2 * VD], attn_t[:, hh, 2 * P:3 * P], v[:, 1, cols], start=False, stop=True).then_inc(pv_done, 1)

            for t in range(2 * PAIRS):
                s = S_Q + t
                if t == 1:
                    pe.wait_ge(v_done, PAIRS)
                elif t < PAIRS:
                    pe.wait_ge(kq_out, (PAIRS + t - 1 if t else PAIRS) * TB)
                for g in range(NG):
                    if t < PAIRS:
                        in_group(s, g, b_tile, PAIR[t % 2])
                    else:
                        if t == PAIRS and g < 2:
                            pe.wait_ge(kq_out, (2 * PAIRS - 1 + g) * TB)
                        else:
                            pe.wait_ge(h_added, H_O + (t - PAIRS) * NG + g - 1)
                        if g == 0:
                            pe.wait_ge(t_taken, 2 * R_ATT[("o", t - PAIRS)] + 2)
                        group(s, g, [o_tile(t - PAIRS, c) for c in range(4)], PAIR[g % 2], True, True)
                    attention(t, g)
                    if t == 2 * PAIRS - 1 and g >= 2:
                        turn_h(2, g - 2, H_MLP[1] - NG + g - 1)

            mlp(1)


_INS = ["x", "mix_norm", "mlp_norm", "pool_w", "pool_scale", "kv_norm", "w_kv", "w_q", "lam", "subln",
        "w_o", "w_mlp_in", "w_mlp_out", "final_norm"]


def kernel(**inputs):
    import concourse.bacc as bacc
    from concourse.bass_utils import run_bass_kernel_spmd

    nc = bacc.Bacc("TRN2", target_bir_lowering=False, num_devices=1)
    arrays = {f"in_{n}": np.ascontiguousarray(inputs[n]) for n in _INS}
    arrays["keep_consts"], arrays["pool_consts"] = shape_constants()
    args = [nc.dram_tensor(n, a.shape, mybir.dt.from_np(a.dtype), kind="ExternalInput").ap() for n, a in arrays.items()]
    out = nc.dram_tensor("out", (1, SEQ, D), F32, kind="ExternalOutput").ap()
    trunk(nc, *args, out)
    return run_bass_kernel_spmd(nc, [arrays], core_ids=[0]).results[0]["out"]
```
